# Optimizing a Trainium2 kernel written in Bass

```python
import math
import jax, jax.numpy as jnp
from jax import lax
import numpy as np

D_MODEL = 2048
BATCH = 1
SEQ = 256
DEPTH = 1

CHUNK = 64
EPS = 1e-6
MIX_WIDTH = D_MODEL
RET_HEAD_DIM = 128
RET_WIDTH = MIX_WIDTH // 2
RET_HEADS = RET_WIDTH // RET_HEAD_DIM
ROPE_BASE = 10000.0
SWA_HEAD_DIM = 64
SWA_WIDTH = MIX_WIDTH - RET_WIDTH
SWA_HEADS = SWA_WIDTH // SWA_HEAD_DIM
SWA_GQA_RATIO = 8
SWA_KV_HEADS = SWA_HEADS // SWA_GQA_RATIO
SWA_WINDOW = 128
WINDOW_CHUNKS = SWA_WINDOW // CHUNK
RET_COLS = 4 * RET_WIDTH
SWA_Q_COLS = SWA_HEADS * SWA_HEAD_DIM
SWA_KV_COLS = SWA_KV_HEADS * SWA_HEAD_DIM
SWA_COLS = SWA_Q_COLS + 2 * SWA_KV_COLS
IN_COLS = RET_COLS + SWA_COLS
D_FF = ((8 * D_MODEL // 3 + 255) // 256) * 256
CONV_WIDTH = 3
NEG_INF = -1e30

kernel_name = "hybrid_retention_swa_sink_convglu"

def rms_norm(x, g):
    xf = x.astype(jnp.float32)
    y = xf * lax.rsqrt(jnp.mean(xf * xf, axis=-1, keepdims=True) + EPS)
    return (y * g.astype(jnp.float32)).astype(x.dtype)

def rotary(x, pos):
    d = x.shape[-1]
    half = d // 2
    inv_freq = ROPE_BASE ** (-jnp.arange(half, dtype=jnp.float32) / half)
    ang = pos[:, None] * inv_freq[None, :]
    cos = jnp.cos(ang)[None, :, None, :]
    sin = jnp.sin(ang)[None, :, None, :]
    xf = x.astype(jnp.float32)
    x1, x2 = xf[..., :half], xf[..., half:]
    return jnp.concatenate([x1 * cos - x2 * sin, x1 * sin + x2 * cos], axis=-1).astype(x.dtype)

def retention(q, k, v, g, gn_gain):
    B, T, H, d = q.shape
    NC = T // CHUNK
    log_gamma = jnp.log1p(-jnp.exp2(-5.0 - jnp.arange(H, dtype=jnp.float32)))
    idx = jnp.arange(CHUNK, dtype=jnp.float32)
    decay_intra = jnp.exp(log_gamma[:, None, None] * jnp.abs(idx[:, None] - idx[None, :]))
    decay_q = jnp.exp((idx[:, None] + 1.0) * log_gamma[None, :])
    decay_k = jnp.exp((CHUNK - 1.0 - idx)[:, None] * log_gamma[None, :])
    decay_chunk = jnp.exp(CHUNK * log_gamma)

    qc = q.reshape(B, NC, CHUNK, H, d)
    kc = k.reshape(B, NC, CHUNK, H, d)
    vc = v.reshape(B, NC, CHUNK, H, d)

    s = jnp.einsum('bnqhd,bnkhd->bnhqk', qc, kc) * decay_intra[None, None]
    o_intra = jnp.einsum('bnhqk,bnkhe->bnqhe', s, vc)

    def step(S, inp):
        qi, ki, vi = inp
        o = jnp.einsum('bqhd,bhde->bqhe', qi, S) * decay_q[None, :, :, None]
        S = S * decay_chunk[None, :, None, None] + jnp.einsum(
            'bkhd,bkhe->bhde', ki * decay_k[None, :, :, None], vi)
        return S, o

    S0 = jnp.zeros((B, H, d, d), jnp.float32)
    xs = (jnp.moveaxis(qc, 1, 0), jnp.moveaxis(kc, 1, 0), jnp.moveaxis(vc, 1, 0))
    _, o_inter = lax.scan(step, S0, xs)
    o = (o_intra + jnp.moveaxis(o_inter, 0, 1)).astype(jnp.float32).reshape(B, T, H, d)

    mu = jnp.mean(o, axis=-1, keepdims=True)
    var = jnp.mean(jnp.square(o - mu), axis=-1, keepdims=True)
    on = ((o - mu) * lax.rsqrt(var + EPS)).reshape(B, T, H * d) * gn_gain.astype(jnp.float32)
    return (jax.nn.silu(g.astype(jnp.float32)) * on).astype(q.dtype)

def swa_sink_attention(q, k, v, sinks):
    B, T, Hq, d = q.shape
    Hkv = k.shape[2]
    G = Hq // Hkv
    NC = T // CHUNK
    W = WINDOW_CHUNKS
    qc = q.reshape(B, NC, CHUNK, Hkv, G, d)
    kc = k.reshape(B, NC, CHUNK, Hkv, d)
    vc = v.reshape(B, NC, CHUNK, Hkv, d)
    pad = ((0, 0), (W - 1, 0), (0, 0), (0, 0), (0, 0))
    kp = jnp.pad(kc, pad)
    vp = jnp.pad(vc, pad)
    kb = jnp.concatenate([kp[:, j:j + NC] for j in range(W)], axis=2)
    vb = jnp.concatenate([vp[:, j:j + NC] for j in range(W)], axis=2)
    key_chunk = jnp.arange(NC)[:, None] - (W - 1) + (jnp.arange(W * CHUNK) // CHUNK)[None, :]
    valid = key_chunk >= 0

    s = jnp.einsum('bnqhgd,bnkhd->bhgnqk', qc, kb).astype(jnp.float32) * (d ** -0.5)
    s = jnp.where(valid[None, None, None, :, None, :], s, NEG_INF)
    sink = sinks.astype(jnp.float32).reshape(Hkv, G)[None, :, :, None, None, None]
    m = jnp.maximum(jnp.max(s, axis=-1, keepdims=True), sink)
    p = jnp.exp(s - m)
    denom = jnp.sum(p, axis=-1, keepdims=True) + jnp.exp(sink - m)
    pn = (p / denom).astype(v.dtype)
    o = jnp.einsum('bhgnqk,bnkhd->bnqhgd', pn, vb)
    return o.reshape(B, T, Hq * d)

def causal_depthwise_conv(a, w, b):
    F = a.shape[-1]
    y = lax.conv_general_dilated(
        a, w.reshape(CONV_WIDTH, 1, F).astype(a.dtype),
        window_strides=(1,), padding=[(CONV_WIDTH - 1, 0)],
        dimension_numbers=('NWC', 'WIO', 'NWC'), feature_group_count=F)
    return y + b

def setup_inputs(seed: int = 0) -> dict:
    key = jax.random.key(seed)
    ks = jax.random.split(key, 13)
    f32 = jnp.float32
    nrm = lambda k, shape: jax.random.normal(k, shape, f32)
    return {
        "x": nrm(ks[0], (BATCH, SEQ, D_MODEL)),
        "ln1": 1.0 + 0.02 * nrm(ks[1], (DEPTH, D_MODEL)),
        "w_in": nrm(ks[2], (DEPTH, D_MODEL, IN_COLS)) * D_MODEL ** -0.5,
        "b_swa": 0.02 * nrm(ks[3], (DEPTH, SWA_COLS)),
        "ret_gn": 1.0 + 0.02 * nrm(ks[4], (DEPTH, RET_WIDTH)),
        "sinks": nrm(ks[5], (DEPTH, SWA_HEADS)),
        "w_out": nrm(ks[6], (DEPTH, MIX_WIDTH, D_MODEL)) * MIX_WIDTH ** -0.5,
        "ln2": 1.0 + 0.02 * nrm(ks[7], (DEPTH, D_MODEL)),
        "w_ffn_in": nrm(ks[8], (DEPTH, D_MODEL, 2 * D_FF)) * D_MODEL ** -0.5,
        "conv_w": nrm(ks[9], (DEPTH, CONV_WIDTH, D_FF)) * CONV_WIDTH ** -0.5,
        "conv_b": 0.02 * nrm(ks[10], (DEPTH, D_FF)),
        "w_ffn_out": nrm(ks[11], (DEPTH, D_FF, D_MODEL)) * D_FF ** -0.5,
        "ln_f": 1.0 + 0.02 * nrm(ks[12], (D_MODEL,)),
    }

def reference(x, ln1, w_in, b_swa, ret_gn, sinks, w_out, ln2, w_ffn_in, conv_w, conv_b, w_ffn_out, ln_f):
    B, T, _ = x.shape
    pos = jnp.arange(T, dtype=jnp.float32)
    for l in range(DEPTH):
        h = rms_norm(x, ln1[l])
        p = h @ w_in[l]
        rq, rk, rv, rg = jnp.split(p[..., :RET_COLS], 4, axis=-1)
        sp = p[..., RET_COLS:] + b_swa[l]
        sq = sp[..., :SWA_Q_COLS]
        sk = sp[..., SWA_Q_COLS:SWA_Q_COLS + SWA_KV_COLS]
        sv = sp[..., SWA_Q_COLS + SWA_KV_COLS:]

        rq = rotary(rq.reshape(B, T, RET_HEADS, RET_HEAD_DIM), pos) * (RET_HEAD_DIM ** -0.5)
        rk = rotary(rk.reshape(B, T, RET_HEADS, RET_HEAD_DIM), pos)
        rv = rv.reshape(B, T, RET_HEADS, RET_HEAD_DIM)
        r_out = retention(rq, rk, rv, rg, ret_gn[l])

        s_out = swa_sink_attention(
            sq.reshape(B, T, SWA_HEADS, SWA_HEAD_DIM),
            sk.reshape(B, T, SWA_KV_HEADS, SWA_HEAD_DIM),
            sv.reshape(B, T, SWA_KV_HEADS, SWA_HEAD_DIM),
            sinks[l])

        mix = jnp.concatenate([r_out, s_out.astype(r_out.dtype)], axis=-1)
        x = x + mix @ w_out[l]

        h = rms_norm(x, ln2[l])
        u = h @ w_ffn_in[l]
        a, b = jnp.split(u, 2, axis=-1)
        a = causal_depthwise_conv(a, conv_w[l], conv_b[l])
        x = x + (jax.nn.gelu(a, approximate=False) * b) @ w_ffn_out[l]
    return rms_norm(x, ln_f)


_drawn_inputs = setup_inputs


def setup_inputs(seed=0):
    import zlib

    import numpy as np

    out = dict(_drawn_inputs(seed))
    spreads = {}
    factors = {'ln1': 2.961,
     'b_swa': 12.85,
     'ret_gn': 6.66,
     'sinks': 64.0,
     'ln2': 10.507,
     'conv_b': 14.99,
     'ln_f': 8.467}
    for name, (base, spread) in spreads.items():
        noise = np.random.default_rng([zlib.crc32(name.encode()), seed]).standard_normal(out[name].shape)
        drawn = base * np.exp(spread * noise) if base else spread * noise
        out[name] = __import__('jax').numpy.asarray(drawn.astype(out[name].dtype))
    for name, factor in factors.items():
        out[name] = (out[name] * factor).astype(out[name].dtype)
    return out
```

```python
from contextlib import ExitStack

import numpy as np

import concourse.bass as bass
from concourse import mybir

F32 = mybir.dt.float32
F32R = mybir.dt.float32r
I32 = mybir.dt.int32
ALU = mybir.AluOpType
ACT = mybir.ActivationFunctionType
AX_X = mybir.AxisListType.X

P = 128
D_MODEL = 2048
SEQ = 256
TOK = SEQ // P
KT = D_MODEL // P
COLS = 512
EPS = 1e-6
CHUNK = 64

RET_HEADS = 8
RET_DIM = 128
RET_WIDTH = RET_HEADS * RET_DIM
SWA_HEADS = 16
SWA_DIM = 64
SWA_KV = 2
PAIRS = SWA_HEADS // 2
SWA_Q0 = 4 * RET_WIDTH
SWA_KV0 = SWA_Q0 + SWA_HEADS * SWA_DIM
KV_COLS = 2 * SWA_KV * SWA_DIM
KEYS1 = 192
D_FF = 5632
GROUPS = D_FF // COLS
FT = COLS // P
BLOCKS = D_MODEL // COLS
NEG = -1e30
ROOT_MAGIC = float(0x5F3759DF)
ROOT_STEPS = 11

RAW = 8
SPLIT = 4
KV_TILE = 0
Q_TILE = KV_TILE + 4
HEAD_TILE = Q_TILE + 16
OUT_TILE = HEAD_TILE + 8 * RET_HEADS
FFN_TILE = OUT_TILE + 8 * BLOCKS
LOOP_TILE = FFN_TILE + 16
GROUP_TILES = 24
LAST_TILE = LOOP_TILE + GROUP_TILES * (GROUPS - 1)
TILES = LAST_TILE + 8

C_LN1, C_LN2, C_GN, C_QB, C_CB = 0, 16, 32, 40, 48
N_ROWS0 = C_CB + D_FF // P
C_W01 = N_ROWS0
C_W2 = C_W01 + 2 * (D_FF // P)
N_COLS = C_W2 + D_FF // P

OUT_ROWS = [(0, 1), (2, 3), (4, 5), (8, 9), (10, 12), (13, 14), (6, 11), (7, 15)]
OUT_NEEDS = [6, 6, 6, 6, 6, 6, 7, 8]
OUT_ORDER = ([(0, t) for t in range(7)] + [(1, t) for t in range(7)] + [(0, 7), (1, 7)]
             + [(b, t) for b in (2, 3) for t in range(8)])


def is_head_tile(n):
    return HEAD_TILE <= n < OUT_TILE


def landed_value(n):
    return 16 * sum(2 if is_head_tile(m) else 1 for m in range(n % RAW, n + 1, RAW))


def build(nc, x, ln1, w_in, b_swa, ret_gn, sinks, w_out, ln2, w_ffn_in, conv_w, conv_b, w_ffn_out,
          ln_f, ident_in, rope_in, mask_in, decay_in, y):
    x_v = x.rearrange("b (t p) d -> (b p) t d", p=P)
    y_v = y.rearrange("b (t p) d -> (b p) t d", p=P)
    w_in_v = w_in.rearrange("l (t p) n -> (l p) t n", p=P)
    w_head_v = w_in[:, :, 0:SWA_Q0].rearrange("l (t p) (g n) -> (l p) t g n", p=P, g=4)
    w_out_v = w_out.rearrange("l (t p) n -> (l p) t n", p=P)
    w_ffn_in_v = w_ffn_in.rearrange("l (t p) n -> (l p) t n", p=P)
    w_ffn_out_v = w_ffn_out.rearrange("l (t p) n -> (l p) t n", p=P)
    b_swa_row = b_swa.rearrange("l n -> (l n)")

    with ExitStack() as ctx:
        def sb(name, shape, dt=F32, scope=ctx):
            return scope.enter_context(nc.sbuf_tensor(name, shape, dt))

        def bank(name):
            return ctx.enter_context(nc.psum_tensor(name, [P, COLS], F32))

        def sem(name):
            return ctx.enter_context(nc.semaphore(name))

        x_res = sb("x_res", [P, TOK, D_MODEL])
        h_hi = sb("h_hi", [P, KT, SEQ], F32R)
        h_lo = sb("h_lo", [P, KT, SEQ], F32R)
        mix_hi = sb("mix_hi", [P, KT, SEQ], F32R)
        mix_lo = sb("mix_lo", [P, KT, SEQ], F32R)
        raw = sb("raw", [P, RAW, 2 * COLS])
        w_hi = sb("w_hi", [P, SPLIT, 2 * COLS], F32R)
        w_lo = sb("w_lo", [P, SPLIT, 2 * COLS], F32R)
        ident = sb("ident", [P, P])
        cols = sb("cols", [P, N_COLS])
        sumsq = sb("sumsq", [P, TOK, BLOCKS])
        sq_sum = sb("sq_sum", [P, TOK])
        meansq = sb("meansq", [P, TOK])
        rstd = sb("rstd", [P, TOK])
        root_y, root_h, root_t = (sb(f"root_{c}", [P, TOK]) for c in "yht")
        g_hi, g_lo = mix_hi[:, 0:FT, :], mix_lo[:, 0:FT, :]

        part1 = ctx.enter_context(ExitStack())

        def s1(name, shape, dt=F32):
            return sb(name, shape, dt, part1)

        rows = s1("rows", [P, 3, P])
        rope = s1("rope", [P, TOK, 2, RET_DIM])
        mask = s1("mask", [P, P + KEYS1])
        decay = s1("decay", [P, RET_HEADS, 2 * P])
        kv_bias = s1("kv_bias", [P, KV_COLS])
        neg_sink = s1("neg_sink", [P, SWA_HEADS])
        proj = s1("proj", [P, 2, TOK, 4, P])
        rot_a = s1("rot_a", [P, TOK, 2, P])
        rot_b = s1("rot_b", [P, TOK, 2, P])
        qk_rot = s1("qk_rot", [P, TOK, 2, P])
        qk_t = s1("qk_t", [P, 2, SEQ])
        ret_p = s1("ret_p", [P, 3 * P])
        o_stats = s1("o_stats", [P, TOK, 6])
        o_mv = s1("o_mv", [P, TOK, 2])
        o_var = s1("o_var", [P, TOK])
        o_rstd = s1("o_rstd", [P, TOK])
        o_norm = s1("o_norm", [P, TOK, P])
        gate_t = s1("gate_t", [P, TOK, P])
        gate = s1("gate", [P, TOK, P])
        mix_tok = s1("mix_tok", [P, TOK, 2, P])
        kv_tok = s1("kv_tok", [P, TOK, KV_COLS])
        k_dup = s1("k_dup", [P, TOK, SWA_KV, 2, SWA_DIM])
        k_diag = s1("k_diag", [P, SWA_KV, 2, SEQ])
        v_shift = s1("v_shift", [P, 2, SWA_KV * SWA_DIM])
        q_t = s1("q_t", [P, PAIRS, SEQ])
        q_now = s1("q_now", [P, 2, SEQ])
        probs = s1("probs", [P, 2 * (P + KEYS1)])
        p_t = s1("p_t", [P, 2, 2, P])
        p_t2 = s1("p_t2", [P, 2, P])
        row_max = s1("row_max", [P, 4])
        neg_max = s1("neg_max", [P, 4])
        sink_in = s1("sink_in", [P, 4])
        sink_e = s1("sink_e", [P, 4])
        p_sum = s1("p_sum", [P, 4])
        denom = s1("denom", [P, 4])
        r_denom = s1("r_denom", [P, 4])
        x_squares = proj[:].rearrange("p a t g n -> p (a t g n)")
        part1.close()

        h_tok = sb("h_tok", [P, TOK, D_MODEL])
        conv = sb("conv", [P, FT, SEQ])
        gated = sb("gated", [P, FT, SEQ])
        lnf_row = sb("lnf_row", [P, D_MODEL])
        squares = gated[:, 0:2, :]

        acc = [[bank(f"acc{i}{t}") for t in range(TOK)] for i in range(2)]
        bank_s0, bank_s1, bank_t, bank_r = bank("bank_s0"), bank("bank_s1"), bank("bank_t"), bank("bank_r")
        turn_banks = [bank_s0, bank_s1, bank_t, bank_r]
        out_banks = [[bank_s0, bank_s1], [bank_t, bank_r]]

        raw_landed = [sem(f"raw_landed{r}") for r in range(RAW)]
        hi_ready = sem("hi_ready")
        lo_ready = sem("lo_ready")
        tile_used = sem("tile_used")
        x_landed = [sem(f"x_landed{t}") for t in range(TOK)]
        ident_landed = sem("ident_landed")
        rows_landed = sem("rows_landed")
        bias_landed = sem("bias_landed")
        sink_landed = sem("sink_landed")
        rope_landed = sem("rope_landed")
        mask_landed = sem("mask_landed")
        decay_landed = sem("decay_landed")
        lnf_landed = sem("lnf_landed")
        shift_landed = sem("shift_landed")
        cols_turned = sem("cols_turned")
        cols_ready = sem("cols_ready")
        gain_ready = sem("gain_ready")
        h_turned = sem("h_turned")
        h_hi_ready = sem("h_hi_ready")
        h_lo_ready = sem("h_lo_ready")
        sumsq_ready = sem("sumsq_ready")
        rstd_ready = sem("rstd_ready")
        kv_ready = sem("kv_ready")
        k_dup_ready = sem("k_dup_ready")
        k_turned = sem("k_turned")
        k_ready = sem("k_ready")
        q_in_sbuf = sem("q_in_sbuf")
        q_turned = sem("q_turned")
        q_ready = sem("q_ready")
        zeroed = sem("zeroed")
        neg_sink_ready = sem("neg_sink_ready")
        head_in_sbuf = sem("head_in_sbuf")
        q_now_ready = sem("q_now_ready")
        scores_done = sem("scores_done")
        masked = sem("masked")
        row_max_ready = sem("row_max_ready")
        neg_max_ready = sem("neg_max_ready")
        sink_in_ready = sem("sink_in_ready")
        probs_ready = sem("probs_ready")
        denom_ready = sem("denom_ready")
        r_denom_ready = sem("r_denom_ready")
        probs_turned = sem("probs_turned")
        p_t_ready = sem("p_t_ready")
        p_t2_ready = sem("p_t2_ready")
        swa_done = sem("swa_done")
        swa_ready = sem("swa_ready")
        rot_a_ready = sem("rot_a_ready")
        rot_b_ready = sem("rot_b_ready")
        rot_ready = sem("rot_ready")
        qk_turned = sem("qk_turned")
        qk_t_ready = sem("qk_t_ready")
        ret_scores_done = sem("ret_scores_done")
        ret_p_ready = sem("ret_p_ready")
        ret_done = sem("ret_done")
        o_stats_ready = sem("o_stats_ready")
        o_mv_ready = sem("o_mv_ready")
        o_var_ready = sem("o_var_ready")
        root_step = sem("root_step")
        o_rstd_ready = sem("o_rstd_ready")
        o_norm_ready = sem("o_norm_ready")
        gate_t_ready = sem("gate_t_ready")
        gate_ready = sem("gate_ready")
        ret_ready = sem("ret_ready")
        mix_turned = sem("mix_turned")
        mix_hi_ready = sem("mix_hi_ready")
        mix_lo_ready = sem("mix_lo_ready")
        out_added = sem("out_added")
        norm_ready = sem("norm_ready")
        norm_ready0 = sem("norm_ready0")
        norm_ready1 = sem("norm_ready1")
        meansq_ready = sem("meansq_ready")
        sq_sum_ready = sem("sq_sum_ready")
        tap2_ready = sem("tap2_ready")
        tap1_ready = sem("tap1_ready")
        conv_ready = sem("conv_ready")
        gelu_ready = sem("gelu_ready")
        gated_ready = sem("gated_ready")
        g_hi_ready = sem("g_hi_ready")
        g_lo_ready = sem("g_lo_ready")
        ffn_added = sem("ffn_added")
        scaled = sem("scaled")
        y_ready = sem("y_ready")
        y_ready2 = sem("y_ready2")
        y_stored = sem("y_stored")

        block = ctx.enter_context(nc.Block())

        @block.sync
        def _(sp):
            def free_raw(n):
                if not isinstance(n, int) or n >= RAW:
                    sp.wait_ge(lo_ready, n - RAW + 1)

            def load(n, slot, source):
                free_raw(n)
                sp.dma_start(raw[:, slot, :].rearrange("p (t n) -> p t n", n=source.shape[-1]),
                             source).then_inc(raw_landed[slot], 16)

            def load_head(n, slot, head, k):
                free_raw(n)
                for q in range(2):
                    sp.dma_start(raw[:, slot, q * COLS:(q + 1) * COLS].rearrange("p (g n) -> p g n", g=4),
                                 w_head_v[:, 2 * k + q, :, bass.ds(head * RET_DIM, RET_DIM)]
                                 ).then_inc(raw_landed[slot], 16)

            def load_kv(n):
                load(n, n % RAW, w_in_v[:, 4 * n:4 * n + 4, SWA_KV0:SWA_KV0 + KV_COLS])

            def load_q(n):
                b, k = divmod(n - Q_TILE, 8)
                load(n, n % RAW, w_in_v[:, 2 * k:2 * k + 2, SWA_Q0 + b * COLS:SWA_Q0 + (b + 1) * COLS])

            def load_out(n):
                b, t = OUT_ORDER[n - OUT_TILE]
                r0, r1 = OUT_ROWS[t]
                load(n, n % RAW, w_out_v[:, r0:r1 + 1:r1 - r0, b * COLS:(b + 1) * COLS])

            def load_up(n, slot, k, first_col):
                load(n, slot, w_ffn_in_v[:, 2 * k:2 * k + 2, bass.ds(first_col, COLS)])

            def load_down(n, slot, group, k):
                c, q = divmod(k, 2)
                load(n, slot, w_ffn_out_v[:, bass.ds(group * FT + 2 * q, 2), c * COLS:(c + 1) * COLS])

            sp.dma_start(ident[:], ident_in).then_inc(ident_landed, 16)
            for t in range(TOK):
                sp.dma_start(x_res[:, t, :], x_v[:, t, :]).then_inc(x_landed[t], 16)
            sp.dma_start(rows[C_LN1:C_LN1 + KT, 0, :], ln1.rearrange("l (r n) -> (l r) n", n=P)).then_inc(rows_landed, 16)
            sp.dma_start(rows[C_LN2:C_LN2 + KT, 0, :], ln2.rearrange("l (r n) -> (l r) n", n=P)).then_inc(rows_landed, 16)
            sp.dma_start(rows[C_GN:C_GN + RET_HEADS, 0, :], ret_gn.rearrange("l (r n) -> (l r) n", n=P)).then_inc(rows_landed, 16)
            sp.dma_start(rows[C_QB:C_QB + PAIRS, 0, :],
                         b_swa_row[0:PAIRS * P].rearrange("(r n) -> r n", n=P)).then_inc(rows_landed, 16)
            sp.dma_start(rows[C_CB:N_ROWS0, 0, :], conv_b.rearrange("l (r n) -> (l r) n", n=P)).then_inc(rows_landed, 16)
            conv_rows = conv_w.rearrange("l w (r n) -> (l w r) n", n=P)
            taps01 = 2 * (D_FF // P)
            sp.dma_start(rows[0:taps01, 1, :], conv_rows[0:taps01, :]).then_inc(rows_landed, 16)
            sp.dma_start(rows[0:D_FF // P, 2, :], conv_rows[taps01:, :]).then_inc(rows_landed, 16)
            for n in range(KV_TILE, Q_TILE):
                load_kv(n)
            sp.dma_start(kv_bias[:], b_swa_row[PAIRS * P:].partition_broadcast(P)).then_inc(bias_landed, 16)
            for n in range(Q_TILE, RAW):
                load_q(n)
            sp.dma_start(neg_sink[:], sinks.rearrange("l n -> (l n)").partition_broadcast(P)).then_inc(sink_landed, 16)
            sp.dma_start(rope[:], rope_in).then_inc(rope_landed, 16)
            sp.dma_start(mask[:], mask_in).then_inc(mask_landed, 16)
            sp.dma_start(decay[:], decay_in).then_inc(decay_landed, 16)
            for n in range(RAW, HEAD_TILE):
                load_q(n)
            v0 = SWA_KV * SWA_DIM
            sp.wait_ge(kv_ready, TOK)
            sp.dma_start(v_shift[0:64, 0, :], kv_tok[64:128, 0, v0:]).then_inc(shift_landed, 16)
            sp.dma_start(v_shift[64:128, 0, :], kv_tok[0:64, 1, v0:]).then_inc(shift_landed, 16)
            sp.dma_start(v_shift[0:64, 1, :], kv_tok[64:128, 1, v0:]).then_inc(shift_landed, 16)
            with sp.Fori(0, RET_HEADS // 2) as i:
                for j in range(2):
                    for k in range(8):
                        n = HEAD_TILE + 8 * j + k
                        load_head(i * 16 + n, n % RAW, i * 2 + j, k)
            for n in range(OUT_TILE, FFN_TILE):
                load_out(n)
            for k in range(8):
                load_up(FFN_TILE + k, (FFN_TILE + k) % RAW, k, 0)
            sp.wait_ge(mix_lo_ready, 2 * RET_HEADS)
            sp.dma_start(lnf_row[:], ln_f.partition_broadcast(P)).then_inc(lnf_landed, 16)
            for k in range(8):
                load_up(FFN_TILE + 8 + k, (FFN_TILE + 8 + k) % RAW, k, D_FF)
            with sp.Fori(0, GROUPS - 1) as f:
                n = LOOP_TILE
                for k in range(8):
                    load_up(f * GROUP_TILES + (n + k), (n + k) % RAW, k, f * COLS + COLS)
                for k in range(8):
                    load_down(f * GROUP_TILES + (n + 8 + k), (n + 8 + k) % RAW, f, k)
                for k in range(8):
                    load_up(f * GROUP_TILES + (n + 16 + k), (n + 16 + k) % RAW, k, f * COLS + (COLS + D_FF))
            for k in range(8):
                load_down(LAST_TILE + k, (LAST_TILE + k) % RAW, GROUPS - 1, k)
            for q in range(2):
                half = slice(q * 2 * COLS, (q + 1) * 2 * COLS)
                sp.wait_ge(y_ready, 2 * q + 2)
                sp.dma_start(y_v[:, 0, half], h_tok[:, 0, half]).then_inc(y_stored, 16)
                sp.wait_ge(y_ready2, 2 * q + 2)
                sp.dma_start(y_v[:, 1, half], h_tok[:, 1, half]).then_inc(y_stored, 16)
            sp.wait_ge(y_stored, 4 * 16)

        @block.tensor
        def _(pe):
            mm, turn = nc.tensor.matmul, nc.tensor.transpose

            def three_pass(out, lhs_hi, lhs_lo, rhs_hi, rhs_lo, first, last):
                mm(out, lhs_hi, rhs_hi, start=first, stop=False, skip_group_check=True)
                mm(out, lhs_hi, rhs_lo, start=False, stop=False, skip_group_check=True)
                return mm(out, lhs_lo, rhs_hi, start=False, stop=last, skip_group_check=True)

            def tile(n, slot, banks, act_hi, act_lo, row_blocks, first, last):
                pe.wait_ge(lo_ready, n + 1)
                width = 2 * COLS // len(row_blocks)
                for q, kt in enumerate(row_blocks):
                    for t in range(TOK):
                        own, w = slice(t * P, (t + 1) * P), slice(q * width, (q + 1) * width)
                        ins = three_pass(banks[t][:, 0:width], act_hi[:, kt, own], act_lo[:, kt, own],
                                         w_hi[:, slot, w], w_lo[:, slot, w],
                                         first and q == 0, last and q == len(row_blocks) - 1)
                ins.then_inc(tile_used, 1)

            def x_turn(g, source, bank_free):
                if g >= 4:
                    pe.wait_ge(h_lo_ready, bank_free + g - 3)
                for q in range(2):
                    for t in range(TOK):
                        c = (2 * g + q) * P
                        ins = turn(turn_banks[g % 4][:, (2 * q + t) * P:(2 * q + t + 1) * P],
                                   source[:, t, c:c + P], ident[:])
                ins.then_inc(h_turned, 1)

            def q_turn(b):
                pe.wait_ge(q_in_sbuf, TOK * (b + 1))
                if b:
                    pe.wait_ge(q_ready, FT)
                for pair in range(4):
                    for t in range(TOK):
                        out = turn_banks[pair // 2][:, (pair % 2) * SEQ + t * P:(pair % 2) * SEQ + (t + 1) * P]
                        ins = turn(out, proj[:, b, t, pair, :], ident[:])
                    ins.then_inc(q_turned, 1)

            pe.wait_ge(ident_landed, 16)
            pe.wait_ge(rows_landed, 16 * 7)
            turn(bank_t[:, 0:N_ROWS0], rows[0:N_ROWS0, 0, :], ident[0:N_ROWS0, 0:N_ROWS0])
            turn(bank_t[:, C_W01:C_W2], rows[0:C_W2 - C_W01, 1, :], ident[0:C_W2 - C_W01, 0:C_W2 - C_W01])
            turn(bank_t[:, C_W2:N_COLS], rows[0:N_COLS - C_W2, 2, :],
                 ident[0:N_COLS - C_W2, 0:N_COLS - C_W2]).then_inc(cols_turned, 1)
            for t in range(TOK):
                pe.wait_ge(x_landed[t], 16)
            for g in (0, 1):
                x_turn(g, x_res, 0)
            pe.wait_ge(cols_ready, 1)
            for g in (2, 3):
                x_turn(g, x_res, 0)
            for m in range(4):
                for g in (4 + 2 * m, 5 + 2 * m):
                    if g < KT // 2:
                        x_turn(g, x_res, 0)
                pe.wait_ge(h_lo_ready, 2 * m + 2)
                tile(KV_TILE + m, m % SPLIT, acc[1], h_hi, h_lo, range(4 * m, 4 * m + 4), m == 0, m == 3)
            for b in range(2):
                if b == 1:
                    pe.wait_ge(kv_ready, TOK)
                for k in range(8):
                    n = Q_TILE + 8 * b + k
                    tile(n, n % SPLIT, acc[b], h_hi, h_lo, (2 * k, 2 * k + 1), k == 0, k == 7)
                    if b == 0 and k == 2:
                        pe.wait_ge(k_dup_ready, 2)
                        for kv in range(SWA_KV):
                            for t in range(TOK):
                                ins = turn(bank_r[:, kv * SEQ + t * P:kv * SEQ + (t + 1) * P],
                                           k_dup[:, t, kv, :, :], ident[:])
                        ins.then_inc(k_turned, 1)
                    if b == 1 and k == 1:
                        q_turn(0)
            for k in range(8):
                n = HEAD_TILE + k
                if k == 0:
                    pe.wait_ge(q_in_sbuf, TOK)
                tile(n, n % SPLIT, acc[0], h_hi, h_lo, (2 * k, 2 * k + 1), k == 0, k == 7)
                if k == 1:
                    q_turn(1)


            def swa_scores(s, j):
                pe.wait_ge(q_now_ready, s + 1)
                mm(bank_s0[:, 0:2 * P], q_now[:, j, 0:P], k_diag[:, j, :, 0:P], start=True, stop=True)
                mm(bank_s1[:, 0:2 * KEYS1], q_now[:, j, P:SEQ], k_diag[:, j, :, SEQ - KEYS1:SEQ],
                   start=True, stop=True).then_inc(scores_done, 1)

            def qk_turn(s):
                pe.wait_ge(rot_ready, s + 1)
                for w in range(2):
                    for t in range(TOK):
                        ins = turn(bank_t[:, w * SEQ + t * P:w * SEQ + (t + 1) * P], qk_rot[:, t, w, :], ident[:])
                ins.then_inc(qk_turned, 1)

            def ret_scores(s):
                pe.wait_ge(qk_t_ready, s + 1)
                mm(bank_r[:, 0:SEQ], qk_t[:, 1, 0:P], qk_t[:, 0, :], start=True, stop=True)
                mm(bank_r[:, SEQ:SEQ + P], qk_t[:, 1, P:SEQ], qk_t[:, 0, P:SEQ],
                   start=True, stop=True).then_inc(ret_scores_done, 1)

            def probs_turn(s):
                pe.wait_ge(probs_ready, s * 5 + 5)
                for a in range(2):
                    turn(bank_s0[:, (2 * a) * P:(2 * a + 1) * P], probs[:, a * P:(a + 1) * P], ident[:])
                    b1 = 2 * P + a * KEYS1
                    turn(bank_s0[:, (2 * a + 1) * P:(2 * a + 2) * P], probs[:, b1:b1 + P], ident[:])
                    ins = turn(bank_s1[0:64, a * P:(a + 1) * P], probs[:, b1 + P:b1 + KEYS1], ident[:])
                ins.then_inc(probs_turned, 1)

            def ret_values(s, j):
                pe.wait_ge(ret_p_ready, s * 2 + 2)
                pe.wait_ge(qk_t_ready, s + 1)
                mm(bank_t[:, 0:P], ret_p[:, 0:P], proj[:, j, 0, 2, :], start=True, stop=True)
                mm(bank_t[:, P:2 * P], ret_p[:, P:2 * P], proj[:, j, 0, 2, :], start=True, stop=False)
                mm(bank_t[:, P:2 * P], ret_p[:, 2 * P:3 * P], proj[:, j, 1, 2, :],
                   start=False, stop=True).then_inc(ret_done, 1)

            def swa_values(s, j):
                pe.wait_ge(p_t_ready, s + 1)
                pe.wait_ge(p_t2_ready, s + 1)
                pe.wait_ge(ret_p_ready, s * 2 + 2)
                if isinstance(s, int) or j == 0:
                    pe.wait_ge(shift_landed, 3 * 16)
                kv = slice(j * SWA_DIM, (j + 1) * SWA_DIM)
                v0 = SWA_KV * SWA_DIM + j * SWA_DIM
                for a in range(2):
                    own0, own1 = a * SWA_DIM, P + a * SWA_DIM
                    mm(bank_r[:, own0:own0 + SWA_DIM], p_t[:, a, 0, :], kv_tok[:, 0, v0:v0 + SWA_DIM],
                       start=True, stop=True)
                    mm(bank_r[:, own1:own1 + SWA_DIM], p_t[:, a, 1, :], v_shift[:, 0, kv], start=True, stop=False)
                    ins = mm(bank_r[:, own1:own1 + SWA_DIM], p_t2[0:64, a, :], v_shift[0:64, 1, kv],
                             start=False, stop=True)
                ins.then_inc(swa_done, 1)

            def mix_turn(s):
                pe.wait_ge(ret_ready, s + 1)
                pe.wait_ge(swa_ready, s + 1)
                for w in range(2):
                    for t in range(TOK):
                        ins = turn(bank_r[:, w * SEQ + t * P:w * SEQ + (t + 1) * P], mix_tok[:, t, w, :], ident[:])
                ins.then_inc(mix_turned, 1)

            def attention_step(s, j, product):
                swa_scores(s, j)
                after = {1: lambda: qk_turn(s), 2: lambda: ret_scores(s), 3: lambda: probs_turn(s),
                         4: lambda: ret_values(s, j), 5: lambda: swa_values(s, j), 7: lambda: mix_turn(s)}
                for k in range(8):
                    product(k)
                    if k in after:
                        after[k]()

            def head_tile(s, j, k):
                n = HEAD_TILE + 8 + 8 * j + k
                tile(s * 8 + (HEAD_TILE + 8 + k), n % SPLIT, acc[1 - j], h_hi, h_lo,
                     (2 * k, 2 * k + 1), k == 0, k == 7)

            def out_tile(n):
                b, t = OUT_ORDER[n - OUT_TILE]
                pe.wait_ge(mix_lo_ready, 2 * OUT_NEEDS[t])
                if t == 0:
                    if b < 2:
                        pe.wait_ge(head_in_sbuf, TOK * (RET_HEADS - 1 + b))
                    else:
                        pe.wait_ge(out_added, TOK * (b - 1))
                tile(n, n % SPLIT, acc[b % 2], mix_hi, mix_lo, OUT_ROWS[t], t == 0, t == 7)

            pe.wait_ge(k_ready, 2)
            with pe.Fori(0, RET_HEADS // 2 - 1) as i:
                for j in range(2):
                    s = i * 2 + j
                    attention_step(s, j, lambda k: head_tile(s, j, k))
            attention_step(RET_HEADS - 2, 0, lambda k: head_tile(RET_HEADS - 2, 0, k))
            attention_step(RET_HEADS - 1, 1, lambda k: out_tile(OUT_TILE + k))
            for n in range(OUT_TILE + 8, FFN_TILE):
                out_tile(n)

            def up_tile(n, slot, banks, k):
                pe.wait_ge(lo_ready, n + 1)
                for q in range(2):
                    for ft in range(FT):
                        w = slice(q * COLS + ft * P, q * COLS + (ft + 1) * P)
                        first = k == 0 and q == 0 and ft % 2 == 0
                        kt = 2 * k + q
                        ins = three_pass(banks[ft // 2][:, (ft % 2) * SEQ:(ft % 2 + 1) * SEQ],
                                         w_hi[:, slot, w], w_lo[:, slot, w], h_hi[:, kt, :], h_lo[:, kt, :],
                                         first, k == 7 and q == 1)
                ins.then_inc(tile_used, 1)

            def up(n, first_slot, banks):
                for k in range(8):
                    up_tile(n + k, (first_slot + k) % SPLIT, banks, k)

            def down(n, first_slot, group):
                for k in range(8):
                    c, q = divmod(k, 2)
                    pe.wait_ge(g_lo_ready, group * 2 + (q + 1))
                    if q == 0 and c >= 2:
                        pe.wait_ge(ffn_added, group * (TOK * BLOCKS) + TOK * (c - 1))
                    tile(n + k, (first_slot + k) % SPLIT, out_banks[c % 2], g_hi, g_lo,
                         (2 * q, 2 * q + 1), q == 0, q == 1)

            for g in range(4):
                pe.wait_ge(norm_ready0, g // 2 + 1)
                pe.wait_ge(norm_ready1, g // 2 + 1)
                x_turn(g, h_tok, KT // 2)
            pe.wait_ge(out_added, TOK * BLOCKS)
            for k in range(8):
                pe.wait_ge(h_lo_ready, KT // 2 + k + 1)
                up_tile(FFN_TILE + k, (FFN_TILE + k) % SPLIT, acc[0], k)
                if k + 4 < KT // 2:
                    pe.wait_ge(norm_ready0, (k + 4) // 2 + 1)
                    pe.wait_ge(norm_ready1, (k + 4) // 2 + 1)
                    x_turn(k + 4, h_tok, KT // 2)
            up(FFN_TILE + 8, 0, acc[1])
            with pe.Fori(0, GROUPS - 1) as f:
                n = f * GROUP_TILES + LOOP_TILE
                pe.wait_ge(conv_ready, f * 2 + 2)
                up(n, LOOP_TILE % SPLIT, acc[0])
                down(n + 8, LOOP_TILE % SPLIT, f)
                pe.wait_ge(gated_ready, f * 2 + 2)
                up(n + 16, LOOP_TILE % SPLIT, acc[1])
            down(LAST_TILE, LAST_TILE % SPLIT, GROUPS - 1)

        @block.scalar
        def _(act):
            run = nc.scalar.activation

            def hi(n, turn=0, tiles=0, landings=0):
                if n >= TILES:
                    return
                act.wait_ge(raw_landed[n % RAW], turn * landings + landed_value(n))
                if n >= SPLIT:
                    act.wait_ge(tile_used, turn * tiles + (n - SPLIT + 1))
                run(w_hi[:, n % SPLIT, :], raw[:, n % RAW, :], ACT.Copy).then_inc(hi_ready, 1)

            def turned_hi(g, column, count):
                act.wait_ge(h_turned, count)
                for q in range(2):
                    kt = 2 * g + q
                    ins = run(h_hi[:, kt, :], turn_banks[g % 4][:, q * SEQ:(q + 1) * SEQ], ACT.Copy,
                              scale=cols[:, column + kt:column + kt + 1])
                ins.then_inc(h_hi_ready, 1)

            def to_sbuf(parity, last_tile, ready):
                act.wait_ge(tile_used, last_tile + 1)
                for t in range(TOK):
                    run(proj[:, parity, t, :, :], acc[parity][t][:].rearrange("p (g n) -> p g n", g=4),
                        ACT.Copy, scale=rstd[:, t:t + 1]).then_inc(ready, 1)

            hi(0)
            act.wait_ge(cols_ready, 1)
            for g in range(KT // 2):
                turned_hi(g, C_LN1, g + 1)
                if g in (1, 3, 5):
                    hi((g + 1) // 2)
            for t in range(TOK):
                hi(SPLIT + t)
                if t:
                    act.wait_ge(sumsq_ready, t)
                run(x_squares, x_res[:, t, :], ACT.Square, accum_out=sumsq[:, t, 0:1]).then_inc(sumsq_ready, 1)
            for n in range(SPLIT + TOK, Q_TILE + 12):
                hi(n)
            act.wait_ge(rstd_ready, 1)
            to_sbuf(0, Q_TILE + 7, q_in_sbuf)
            for n in range(Q_TILE + 12, HEAD_TILE + 4):
                hi(n)
            to_sbuf(1, Q_TILE + 15, q_in_sbuf)
            for n in range(HEAD_TILE + 4, HEAD_TILE + 12):
                hi(n)
            act.wait_ge(q_turned, PAIRS)
            to_sbuf(0, HEAD_TILE + 7, head_in_sbuf)

            def tanh_gate(s, j):
                act.wait_ge(head_in_sbuf, s * TOK + TOK)
                run(gate_t[:], proj[:, j, :, 3, :], ACT.Tanh, scale=0.5).then_inc(gate_t_ready, 1)

            def exp_scores(s):
                act.wait_ge(sink_in_ready, s + 1)
                for c in range(4):
                    b, a = divmod(c, 2)
                    width = KEYS1 if b else P
                    own = slice(b * 2 * P + a * width, b * 2 * P + (a + 1) * width)
                    run(probs[:, own], probs[:, own], ACT.Exp, bias=neg_max[:, c:c + 1],
                        accum_out=p_sum[:, c:c + 1]).then_inc(probs_ready, 1)
                run(sink_e[:], sink_in[:], ACT.Exp).then_inc(probs_ready, 1)

            def qk_out(s):
                act.wait_ge(qk_turned, s + 1)
                run(qk_t[:], bank_t[:].rearrange("p (w n) -> p w n", w=2), ACT.Copy).then_inc(qk_t_ready, 1)

            def probs_out(s):
                act.wait_ge(probs_turned, s + 1)
                run(p_t[:], bank_s0[:].rearrange("p (a b n) -> p a b n", a=2, b=2), ACT.Copy).then_inc(p_t_ready, 1)

            def mix_out(s, pair):
                act.wait_ge(mix_turned, s + 1)
                run(mix_hi[:, bass.ds(s, 1), :], bank_r[:, 0:SEQ].rearrange("p (o n) -> p o n", o=1), ACT.Copy,
                    scale=cols[:, bass.ds(s + C_GN, 1)]).then_inc(mix_hi_ready, 1)
                run(mix_hi[:, bass.ds(pair + RET_HEADS, 1), :],
                    bank_r[:, SEQ:2 * SEQ].rearrange("p (o n) -> p o n", o=1), ACT.Copy).then_inc(mix_hi_ready, 1)

            def attention_step(s, j, pair, split, last):
                split(0)
                tanh_gate(s, j)
                exp_scores(s)
                split(1)
                qk_out(s)
                split(2)
                split(3)
                probs_out(s)
                for k in range(4, 8):
                    split(k)
                if not last:
                    act.wait_ge(ret_done, s + 1)
                    to_sbuf(1 - j, s * 8 + (HEAD_TILE + 15), head_in_sbuf)
                mix_out(s, pair)

            ahead = HEAD_TILE + 8 + SPLIT
            with act.Fori(0, RET_HEADS // 2 - 1) as i:
                for j in range(2):
                    attention_step(i * 2 + j, j, i + 4 * j, lambda k: hi(ahead + 8 * j + k, i, 16, 64), False)
            for s in (RET_HEADS - 2, RET_HEADS - 1):
                attention_step(s, s % 2, s // 2 + 4 * (s % 2), lambda k: hi(ahead + 8 * s + k), s == RET_HEADS - 1)

            def square_sums(b, added, count, before):
                for t in range(TOK):
                    act.wait_ge(added, count + t + 1)
                    act.wait_ge(sumsq_ready, before + TOK * b + t)
                    run(squares, x_res[:, t, b * COLS:(b + 1) * COLS].rearrange("p (a n) -> p a n", a=2),
                        ACT.Square, accum_out=sumsq[:, t, b:b + 1]).then_inc(sumsq_ready, 1)

            for n in range(OUT_TILE + 8, FFN_TILE):
                hi(n + SPLIT)
                b, t = OUT_ORDER[n - OUT_TILE]
                if t == 7:
                    square_sums(b, out_added, TOK * b, TOK)
            act.wait_ge(rstd_ready, 2)
            for c in range(BLOCKS):
                own = slice(c * COLS, (c + 1) * COLS)
                run(h_tok[:, 0, own], x_res[:, 0, own], ACT.Copy, scale=rstd[:, 0:1]).then_inc(norm_ready0, 1)
            for g in range(KT // 2):
                if g >= 4:
                    hi(FFN_TILE + g)
                turned_hi(g, C_LN2, KT // 2 + g + 1)

            def tap2(group):
                for half in range(2):
                    for ft in (2 * half, 2 * half + 1):
                        ins = run(conv[:, ft, :], acc[0][half][:, (ft % 2) * SEQ:(ft % 2 + 1) * SEQ], ACT.Copy,
                                  scale=cols[:, bass.ds(group * FT + (C_W2 + ft), 1)])
                    ins.then_inc(tap2_ready, 1)

            def gelu(group):
                for half in range(2):
                    act.wait_ge(conv_ready, group * 2 + (half + 1))
                    for ft in (2 * half, 2 * half + 1):
                        ins = run(conv[:, ft, :], conv[:, ft, :], ACT.Gelu,
                                  bias=cols[:, bass.ds(group * FT + (C_CB + ft), 1)])
                    ins.then_inc(gelu_ready, 1)

            def g_round(group):
                for half in range(2):
                    own = slice(2 * half, 2 * half + 2)
                    act.wait_ge(gated_ready, group * 2 + (half + 1))
                    run(g_hi[:, own, :], gated[:, own, :], ACT.Copy).then_inc(g_hi_ready, 1)

            for n in range(FFN_TILE + 4, FFN_TILE + 8):
                hi(n + SPLIT)
            act.wait_ge(tile_used, FFN_TILE + 8)
            tap2(0)
            hi(FFN_TILE + 8 + SPLIT)
            gelu(0)
            for n in range(FFN_TILE + 9, LOOP_TILE):
                hi(n + SPLIT)
            with act.Fori(0, GROUPS - 1) as f:
                for k in range(GROUP_TILES):
                    if k == 0:
                        g_round(f)
                    hi(LOOP_TILE + k + SPLIT, f, GROUP_TILES, 3 * 16)
                    if k == 7:
                        act.wait_ge(tile_used, f * GROUP_TILES + (LOOP_TILE + 8))
                        tap2(f + 1)
                    if k == 8:
                        gelu(f + 1)
            g_round(GROUPS - 1)
            for k in range(8):
                hi(LAST_TILE + k + SPLIT)
                if k % 2:
                    square_sums(k // 2, ffn_added, TOK * BLOCKS * (GROUPS - 1) + TOK * (k // 2),
                                TOK + TOK * BLOCKS)
            act.wait_ge(rstd_ready, 3)
            for c in range(BLOCKS):
                own = slice(c * COLS, (c + 1) * COLS)
                act.wait_ge(scaled, TOK * c + 1)
                run(h_tok[:, 0, own], h_tok[:, 0, own], ACT.Copy, scale=rstd[:, 0:1]).then_inc(y_ready, 1)

        @block.vector
        def _(dve):
            tt, ts, stt = nc.vector.tensor_tensor, nc.vector.tensor_scalar, nc.vector.scalar_tensor_tensor

            def lo(n, turn=0, tiles=0):
                if n >= TILES:
                    return
                dve.wait_ge(hi_ready, turn * tiles + (n + 1))
                tt(w_lo[:, n % SPLIT, :], raw[:, n % RAW, :], w_hi[:, n % SPLIT, :].bitcast(F32),
                   ALU.subtract).then_inc(lo_ready, 1)

            def turned_lo(g, column, count):
                dve.wait_ge(h_hi_ready, count)
                for q in range(2):
                    kt = 2 * g + q
                    ins = stt(out=h_lo[:, kt, :], in0=turn_banks[g % 4][:, q * SEQ:(q + 1) * SEQ],
                              scalar=cols[:, column + kt:column + kt + 1], in1=h_hi[:, kt, :].bitcast(F32),
                              op0=ALU.mult, op1=ALU.subtract)
                ins.then_inc(h_lo_ready, 1)

            def inverse_root(call, value, out, last_done):
                steps = 0

                def then_wait(ins):
                    nonlocal steps
                    steps += 1
                    ins.then_inc(root_step, 1)
                    dve.wait_ge(root_step, call * ROOT_STEPS + steps)

                then_wait(ts(root_y[:].bitcast(I32), value.bitcast(I32), 1, None, ALU.arith_shift_right))
                then_wait(ts(root_y[:].bitcast(I32), root_y[:].bitcast(I32), -1.0, ROOT_MAGIC, ALU.mult, ALU.add))
                then_wait(ts(root_h[:], value, -0.5, None, ALU.mult))
                for newton in range(3):
                    then_wait(tt(root_t[:], root_y[:], root_y[:], ALU.mult))
                    then_wait(tt(root_t[:], root_t[:], root_h[:], ALU.mult))
                    if newton < 2:
                        then_wait(stt(out=root_y[:], in0=root_t[:], scalar=1.5, in1=root_y[:],
                                      op0=ALU.add, op1=ALU.mult))
                assert steps == ROOT_STEPS
                stt(out=out, in0=root_t[:], scalar=1.5, in1=root_y[:],
                    op0=ALU.add, op1=ALU.mult).then_inc(last_done, 1)

            def inverse_rms(sums, squares_counted, which):
                dve.wait_ge(sumsq_ready, squares_counted)
                if sums is None:
                    nc.vector.reduce_sum(sq_sum[:], sumsq[:], AX_X).then_inc(sq_sum_ready, 1)
                    dve.wait_ge(sq_sum_ready, which - 1)
                    sums = sq_sum[:]
                ts(meansq[:], sums, 1.0 / D_MODEL, EPS, ALU.mult, ALU.add).then_inc(meansq_ready, 1)
                dve.wait_ge(meansq_ready, which)
                inverse_root(0 if which == 1 else RET_HEADS + which - 1, meansq[:], rstd[:], rstd_ready)

            dve.wait_ge(cols_turned, 1)
            nc.vector.tensor_copy(cols[:], bank_t[:, 0:N_COLS]).then_inc(cols_ready, 1)
            dve.wait_ge(cols_ready, 1)
            ts(cols[:, C_GN:C_GN + RET_HEADS], cols[:, C_GN:C_GN + RET_HEADS], 0.5, None,
               ALU.mult).then_inc(gain_ready, 1)
            lo(0)
            for g in range(KT // 2):
                turned_lo(g, C_LN1, g + 1)
                if g in (1, 3, 5):
                    lo((g + 1) // 2)
            for n in range(4, 7):
                lo(n)
            inverse_rms(sumsq[:, :, 0], TOK, 1)
            lo(7)
            dve.wait_ge(tile_used, Q_TILE)
            dve.wait_ge(bias_landed, 16)
            dve.wait_ge(rstd_ready, 1)
            for t in range(TOK):
                stt(out=kv_tok[:, t, :], in0=acc[1][t][:, 0:KV_COLS], scalar=rstd[:, t:t + 1], in1=kv_bias[:],
                    op0=ALU.mult, op1=ALU.add).then_inc(kv_ready, 1)
            dve.wait_ge(kv_ready, TOK)
            for d in range(2):
                nc.vector.tensor_copy(k_dup[:, :, :, d, :],
                                      kv_tok[:, :, 0:SWA_KV * SWA_DIM].rearrange("p t (v d) -> p t v d", v=SWA_KV)
                                      ).then_inc(k_dup_ready, 1)
            for n in range(8, 11):
                lo(n)
            dve.wait_ge(k_turned, 1)
            dve.wait_ge(zeroed, 1)
            for half in range(2):
                own = slice(64 * half, 64 * half + 64)
                nc.vector.tensor_copy(k_diag[own, :, half, :],
                                      bank_r[own, :].rearrange("p (v n) -> p v n", v=SWA_KV)).then_inc(k_ready, 1)

            def q_out(b):
                for pair in range(4 * b, 4 * b + 4):
                    dve.wait_ge(q_turned, 4 * b + 4)
                    c = pair % 2 * SEQ
                    ts(q_t[:, pair, :], turn_banks[pair % 4 // 2][:, c:c + SEQ],
                       cols[:, C_QB + pair:C_QB + pair + 1], SWA_DIM ** -0.5, ALU.add, ALU.mult).then_inc(q_ready, 1)

            for n in range(11, 18):
                lo(n)
            q_out(0)
            for n in range(18, 26):
                lo(n)
            q_out(1)
            dve.wait_ge(sink_landed, 16)
            ts(neg_sink[:], neg_sink[:], -1.0, None, ALU.mult).then_inc(neg_sink_ready, 1)
            for n in range(26, HEAD_TILE + 12):
                lo(n)
            dve.wait_ge(neg_sink_ready, 1)
            dve.wait_ge(gain_ready, 1)
            dve.wait_ge(mask_landed, 16)
            dve.wait_ge(rope_landed, 16)
            dve.wait_ge(decay_landed, 16)

            def mask_scores(s):
                dve.wait_ge(scores_done, s + 1)
                parts = ((bank_s0, 0, 0, P), (bank_s1, 2 * P, P, KEYS1))
                for b, at, m, width in parts:
                    tt(probs[:, at:at + 2 * width].rearrange("p (a n) -> p a n", a=2),
                       b[:, 0:2 * width].rearrange("p (a n) -> p a n", a=2),
                       mask[:, m:m + width].unsqueeze(1).broadcast_to([P, 2, width]), ALU.add).then_inc(masked, 1)

            def score_max(s, pair):
                dve.wait_ge(masked, s * 2 + 2)
                for b, (at, width) in enumerate(((0, P), (2 * P, KEYS1))):
                    nc.vector.reduce_max(row_max[:, 2 * b:2 * b + 2],
                                         probs[:, at:at + 2 * width].rearrange("p (a n) -> p a n", a=2),
                                         AX_X).then_inc(row_max_ready, 1)
                sinks2 = neg_sink[:, bass.ds(pair * 2, 2)].unsqueeze(1).broadcast_to([P, TOK, 2])
                dve.wait_ge(row_max_ready, s * 2 + 2)
                stt(out=neg_max[:].rearrange("p (b a) -> p b a", b=TOK),
                    in0=row_max[:].rearrange("p (b a) -> p b a", b=TOK), scalar=-1.0, in1=sinks2,
                    op0=ALU.mult, op1=ALU.min).then_inc(neg_max_ready, 1)
                dve.wait_ge(neg_max_ready, s + 1)
                tt(sink_in[:].rearrange("p (b a) -> p b a", b=TOK),
                   neg_max[:].rearrange("p (b a) -> p b a", b=TOK), sinks2, ALU.subtract).then_inc(sink_in_ready, 1)

            def rotate(s, j):
                dve.wait_ge(head_in_sbuf, s * TOK + TOK)
                tt(rot_a[:], proj[:, j, :, 0:2, :],
                   rope[:, :, 0:1, :].broadcast_to([P, TOK, 2, P]), ALU.mult).then_inc(rot_a_ready, 1)
                dve.wait_ge(rot_a_ready, s + 1)
                dve.wait_ge(rot_b_ready, s * 4 + 4)
                tt(qk_rot[:], rot_a[:], rot_b[:], ALU.add).then_inc(rot_ready, 1)

            def swish(s, j):
                dve.wait_ge(gate_t_ready, s + 1)
                stt(out=gate[:], in0=gate_t[:], scalar=1.0, in1=proj[:, j, :, 3, :],
                    op0=ALU.add, op1=ALU.mult).then_inc(gate_ready, 1)

            def denominators(s):
                dve.wait_ge(probs_ready, s * 5 + 5)
                tt(denom[:], p_sum[:], sink_e[:], ALU.add).then_inc(denom_ready, 1)
                dve.wait_ge(denom_ready, s + 1)
                nc.vector.reciprocal(r_denom[:], denom[:]).then_inc(r_denom_ready, 1)

            def decay_scores(s):
                dve.wait_ge(ret_scores_done, s + 1)
                tt(ret_p[:, 0:2 * P].unsqueeze(1), bank_r[:, 0:2 * P].unsqueeze(1), decay[:, bass.ds(s, 1), :],
                   ALU.mult).then_inc(ret_p_ready, 1)
                tt(ret_p[:, 2 * P:3 * P].unsqueeze(1), bank_r[:, 2 * P:3 * P].unsqueeze(1),
                   decay[:, bass.ds(s, 1), 0:P], ALU.mult).then_inc(ret_p_ready, 1)

            def probs_out(s):
                dve.wait_ge(probs_turned, s + 1)
                nc.vector.tensor_copy(p_t2[0:64, :, :],
                                      bank_s1[0:64, 0:2 * P].rearrange("p (a n) -> p a n", a=2)).then_inc(p_t2_ready, 1)

            def group_norm(s):
                dve.wait_ge(ret_done, s + 1)
                for t in range(TOK):
                    nc.vector.bn_stats(o_stats[:, t, :], bank_t[:, t * P:(t + 1) * P]).then_inc(o_stats_ready, 1)
                dve.wait_ge(o_stats_ready, s * 2 + 2)
                denominators(s)
                for t in range(TOK):
                    nc.vector.bn_aggr(o_mv[:, t, :], o_stats[:, t, :]).then_inc(o_mv_ready, 1)
                dve.wait_ge(o_mv_ready, s * 2 + 2)
                ts(o_var[:], o_mv[:, :, 1], EPS, None, ALU.add).then_inc(o_var_ready, 1)
                dve.wait_ge(o_var_ready, s + 1)
                inverse_root(s + 1, o_var[:], o_rstd[:], o_rstd_ready)
                dve.wait_ge(o_rstd_ready, s + 1)
                for t in range(TOK):
                    ts(o_norm[:, t, :], bank_t[:, t * P:(t + 1) * P], o_mv[:, t, 0:1], o_rstd[:, t:t + 1],
                       ALU.subtract, ALU.mult).then_inc(o_norm_ready, 1)

            def swa_out(s):
                dve.wait_ge(swa_done, s + 1)
                dve.wait_ge(r_denom_ready, s + 1)
                tt(mix_tok[:, :, 1, :].rearrange("p b (a d) -> p b a d", a=2),
                   bank_r[:, 0:2 * P].rearrange("p (b a d) -> p b a d", b=TOK, a=2),
                   r_denom[:].rearrange("p (b a) -> p b a", b=TOK).unsqueeze(3).broadcast_to([P, TOK, 2, SWA_DIM]),
                   ALU.mult).then_inc(swa_ready, 1)

            def mix_out(s, pair):
                dve.wait_ge(mix_hi_ready, s * 2 + 2)
                own, other = bass.ds(s, 1), bass.ds(pair + RET_HEADS, 1)
                stt(out=mix_lo[:, own, :], in0=bank_r[:, 0:SEQ].unsqueeze(1), scalar=cols[:, bass.ds(s + C_GN, 1)],
                    in1=mix_hi[:, own, :].bitcast(F32), op0=ALU.mult, op1=ALU.subtract).then_inc(mix_lo_ready, 1)
                tt(mix_lo[:, other, :], bank_r[:, SEQ:2 * SEQ].unsqueeze(1), mix_hi[:, other, :].bitcast(F32),
                   ALU.subtract).then_inc(mix_lo_ready, 1)

            def attention_step(s, j, pair, split):
                mask_scores(s)
                score_max(s, pair)
                split(0)
                rotate(s, j)
                swish(s, j)
                split(1)
                split(2)
                decay_scores(s)
                split(3)
                probs_out(s)
                split(4)
                group_norm(s)
                split(5)
                swa_out(s)
                split(6)
                split(7)
                mix_out(s, pair)

            ahead = HEAD_TILE + 8 + SPLIT
            with dve.Fori(0, RET_HEADS // 2 - 1) as i:
                for j in range(2):
                    attention_step(i * 2 + j, j, i + 4 * j, lambda k: lo(ahead + 8 * j + k, i, 16))
            for s in (RET_HEADS - 2, RET_HEADS - 1):
                attention_step(s, s % 2, s // 2 + 4 * (s % 2), lambda k: lo(ahead + 8 * s + k))

            def add_block(b, last_tile, banks, added):
                dve.wait_ge(tile_used, last_tile + 1)
                for t in range(TOK):
                    own = x_res[:, t, b * COLS:(b + 1) * COLS]
                    tt(own, own, banks[t][:], ALU.add).then_inc(added, 1)

            for n in range(OUT_TILE + 8, FFN_TILE):
                lo(n + SPLIT)
                b, t = OUT_ORDER[n - OUT_TILE]
                if t == 7:
                    add_block(b, n, acc[b % 2], out_added)
            inverse_rms(None, TOK + TOK * BLOCKS, 2)
            dve.wait_ge(rstd_ready, 2)
            for c in range(BLOCKS):
                own = slice(c * COLS, (c + 1) * COLS)
                ts(h_tok[:, 1, own], x_res[:, 1, own], rstd[:, 1:2], None, ALU.mult).then_inc(norm_ready1, 1)
            for g in range(KT // 2):
                if g >= 4:
                    lo(FFN_TILE + g)
                turned_lo(g, C_LN2, KT // 2 + g + 1)

            def taps(group):
                for half in range(2):
                    dve.wait_ge(tap2_ready, group * 2 + (half + 1))
                    for tap in (1, 0):
                        for ft in (2 * half, 2 * half + 1):
                            back = 2 - tap
                            if tap == 0:
                                dve.wait_ge(tap1_ready, group * 4 + (ft + 1))
                            a = acc[0][half][:, (ft % 2) * SEQ:(ft % 2 + 1) * SEQ - back]
                            ins = stt(out=conv[:, ft, back:SEQ], in0=a,
                                      scalar=cols[:, bass.ds(group * FT + (C_W01 + tap * (D_FF // P) + ft), 1)],
                                      in1=conv[:, ft, back:SEQ], op0=ALU.mult, op1=ALU.add)
                            if tap == 1:
                                ins.then_inc(tap1_ready, 1)
                    ins.then_inc(conv_ready, 1)

            def gate_hidden(group):
                for half in range(2):
                    own = slice(2 * half, 2 * half + 2)
                    dve.wait_ge(gelu_ready, group * 2 + (half + 1))
                    tt(gated[:, own, :], acc[1][half][:].rearrange("p (a n) -> p a n", a=2), conv[:, own, :],
                       ALU.mult).then_inc(gated_ready, 1)

            def g_rest(group):
                for half in range(2):
                    own = slice(2 * half, 2 * half + 2)
                    dve.wait_ge(g_hi_ready, group * 2 + (half + 1))
                    tt(g_lo[:, own, :], gated[:, own, :], g_hi[:, own, :].bitcast(F32),
                       ALU.subtract).then_inc(g_lo_ready, 1)

            for n in range(FFN_TILE + 4, FFN_TILE + 8):
                lo(n + SPLIT)
            taps(0)
            for n in range(FFN_TILE + 8, LOOP_TILE):
                lo(n + SPLIT)
            with dve.Fori(0, GROUPS - 1) as f:
                dve.wait_ge(tile_used, f * GROUP_TILES + LOOP_TILE)
                gate_hidden(f)
                for k in range(GROUP_TILES):
                    lo(LOOP_TILE + k + SPLIT, f, GROUP_TILES)
                    if k == 1:
                        g_rest(f)
                    if k == 7:
                        taps(f + 1)
                    if k in (9, 11, 13, 15):
                        c = (k - 9) // 2
                        add_block(c, f * GROUP_TILES + (LOOP_TILE + k), out_banks[c % 2], ffn_added)
            dve.wait_ge(tile_used, LAST_TILE)
            gate_hidden(GROUPS - 1)
            g_rest(GROUPS - 1)
            dve.wait_ge(lnf_landed, 16)
            for k in range(8):
                lo(LAST_TILE + k + SPLIT)
                if k % 2:
                    c = k // 2
                    own = slice(c * COLS, (c + 1) * COLS)
                    add_block(c, LAST_TILE + k, out_banks[c % 2], ffn_added)
                    for t in range(TOK):
                        dve.wait_ge(ffn_added, TOK * BLOCKS * (GROUPS - 1) + TOK * c + t + 1)
                        tt(h_tok[:, t, own], x_res[:, t, own], lnf_row[:, own], ALU.mult).then_inc(scaled, 1)
            inverse_rms(None, TOK + 2 * TOK * BLOCKS, 3)
            dve.wait_ge(rstd_ready, 3)
            for c in range(BLOCKS):
                own = slice(c * COLS, (c + 1) * COLS)
                dve.wait_ge(scaled, TOK * c + 2)
                ts(h_tok[:, 1, own], h_tok[:, 1, own], rstd[:, 1:2], None, ALU.mult).then_inc(y_ready2, 1)

        @block.gpsimd
        def _(pool):
            def query_copy(j, pair):
                nc.gpsimd.tensor_copy(q_now[:, j, :].unsqueeze(1), q_t[:, bass.ds(pair, 1), :]).then_inc(q_now_ready, 1)

            def attention_step(s, j, next_pair):
                pool.wait_ge(head_in_sbuf, s * TOK + TOK)
                for t in range(TOK):
                    for half in range(2):
                        own, other = slice(64 * half, 64 * half + 64), slice(64 - 64 * half, 128 - 64 * half)
                        nc.gpsimd.tensor_tensor(rot_b[:, t, :, own], proj[:, j, t, 0:2, other],
                                                rope[:, t, 1:2, own].broadcast_to([P, 2, 64]),
                                                ALU.mult).then_inc(rot_b_ready, 1)
                if next_pair is not None:
                    pool.wait_ge(scores_done, s + 1)
                    query_copy(1 - j, next_pair)
                pool.wait_ge(gate_ready, s + 1)
                pool.wait_ge(o_norm_ready, s * 2 + 2)
                nc.gpsimd.tensor_tensor(mix_tok[:, :, 0, :], gate[:], o_norm[:], ALU.mult).then_inc(ret_ready, 1)

            nc.gpsimd.memset(k_diag[:], 0.0).then_inc(zeroed, 1)
            pool.wait_ge(q_ready, PAIRS)
            query_copy(0, 0)
            pool.wait_ge(rope_landed, 16)
            with pool.Fori(0, RET_HEADS // 2 - 1) as i:
                attention_step(i * 2, 0, i + 4)
                attention_step(i * 2 + 1, 1, i + 1)
            attention_step(RET_HEADS - 2, 0, PAIRS - 1)
            attention_step(RET_HEADS - 1, 1, None)


def tables():
    half = RET_DIM // 2
    freq = 10000.0 ** (-np.arange(half, dtype=np.float64) / half)
    angle = (np.arange(SEQ)[:, None] * freq[None, :]).reshape(TOK, P, half).transpose(1, 0, 2)
    cos, sin = np.cos(angle), np.sin(angle)
    rope = np.stack([np.concatenate([cos, cos], -1), np.concatenate([-sin, sin], -1)], 2)

    query, key = np.arange(SEQ)[:, None] // CHUNK, np.arange(SEQ)[None, :] // CHUNK
    seen = (key <= query) & (key >= query - 1)
    mask = np.where(seen, 0.0, NEG)
    mask = np.concatenate([mask[0:P, 0:P], mask[P:, SEQ - KEYS1:]], 1)

    log_gamma = np.log1p(-np.exp2(-5.0 - np.arange(RET_HEADS)))
    k, q = np.arange(P)[:, None], np.arange(SEQ)[None, :]
    visible = q // CHUNK >= k // CHUNK
    decay = np.exp(log_gamma[:, None, None] * np.abs(q - k)) * visible * RET_DIM ** -0.5
    return (np.eye(P, dtype=np.float32), rope.astype(np.float32), mask.astype(np.float32),
            np.ascontiguousarray(decay.transpose(1, 0, 2)).astype(np.float32))


_INS = ["x", "ln1", "w_in", "b_swa", "ret_gn", "sinks", "w_out", "ln2", "w_ffn_in", "conv_w", "conv_b",
        "w_ffn_out", "ln_f"]


def kernel(**inputs):
    import concourse.bacc as bacc
    from concourse.bass_utils import run_bass_kernel_spmd

    nc = bacc.Bacc("TRN2", target_bir_lowering=False, num_devices=1)
    arrays = {f"in_{name}": np.ascontiguousarray(inputs[name]) for name in _INS}
    for name, table in zip(("ident", "rope", "mask", "decay"), tables()):
        arrays[f"table_{name}"] = table
    args = [nc.dram_tensor(name, a.shape, mybir.dt.from_np(a.dtype), kind="ExternalInput").ap()
            for name, a in arrays.items()]
    out = nc.dram_tensor("out_y", (1, SEQ, D_MODEL), F32, kind="ExternalOutput").ap()
    build(nc, *args, out)
    result = run_bass_kernel_spmd(nc, [arrays], core_ids=[0])
    return result.results[0]["out_y"]
```
